# Optimizing a Trainium2 kernel written in Bass

```python
import math
import jax, jax.numpy as jnp
from jax import lax
import numpy as np

D_MODEL = 2048
BATCH = 1
SEQ = 512
DEPTH = 1

CHUNK = 64
D_MIX = D_MODEL
SB_HEADS = 8
SB_HEAD_DIM = 128
D_SB = SB_HEADS * SB_HEAD_DIM
POOL_WINDOWS = (2, 4, 8, 16)
POOL_GROUPS = len(POOL_WINDOWS)
D_POOL = D_MIX - D_SB
POOL_GROUP = D_POOL // POOL_GROUPS
D_IN = 4 * D_SB + 2 * D_POOL
Q_BLOCK = 128
EPS = 1e-6

kernel_name = "hybrid_stickbreak_pool_block"

def _rmsnorm(x, gain):
    x32 = x.astype(jnp.float32)
    y = x32 * lax.rsqrt(jnp.mean(x32 * x32, axis=-1, keepdims=True) + EPS)
    return (y * gain.astype(jnp.float32)).astype(x.dtype)

def _stick_breaking(q, k, v):
    b, h, s, dh = q.shape
    nb = s // Q_BLOCK
    scale = 1.0 / math.sqrt(dh)
    k_pos = jnp.arange(s, dtype=jnp.int32)
    q_blocks = q.reshape(b, h, nb, Q_BLOCK, dh).transpose(2, 0, 1, 3, 4)
    starts = jnp.arange(nb, dtype=jnp.int32) * Q_BLOCK

    def block(args):
        q_blk, start = args
        q_pos = start + jnp.arange(Q_BLOCK, dtype=jnp.int32)
        z = jnp.einsum('bhqd,bhkd->bhqk', q_blk, k,
                       preferred_element_type=jnp.float32) * scale
        mask = k_pos[None, :] < q_pos[:, None]
        log_keep = jnp.where(mask, jax.nn.log_sigmoid(-z), 0.0)
        log_after = lax.cumsum(log_keep, axis=3, reverse=True) - log_keep
        a = jnp.where(mask, jnp.exp(jax.nn.log_sigmoid(z) + log_after), 0.0)
        return jnp.einsum('bhqk,bhkd->bhqd', a.astype(v.dtype), v)

    out = lax.map(block, (q_blocks, starts))
    return out.transpose(1, 2, 0, 3, 4).reshape(b, h, s, dh)

def _multiscale_pool(u, w_pool, pool_scale):
    b, s, _ = u.shape
    u32 = u.astype(jnp.float32)
    c = jnp.cumsum(u32, axis=1)
    t = jnp.arange(s, dtype=jnp.int32)
    outs = []
    for g, w in enumerate(POOL_WINDOWS):
        sl = slice(g * POOL_GROUP, (g + 1) * POOL_GROUP)
        cg = c[:, :, sl]
        lag = jnp.pad(cg[:, :s - w], ((0, 0), (w, 0), (0, 0)))
        count = jnp.minimum(t + 1, w).astype(jnp.float32)[None, :, None]
        mixed = (cg - lag) / count - u32[:, :, sl]
        outs.append(jnp.einsum('bsc,cd->bsd', mixed, w_pool[g].astype(jnp.float32)))
    y = jnp.concatenate(outs, axis=-1) * pool_scale.astype(jnp.float32)
    return y.astype(u.dtype)

def setup_inputs(seed: int = 0) -> dict:
    key = jax.random.key(seed)
    ks = jax.random.split(key, 8)
    x = jax.random.normal(ks[0], (BATCH, SEQ, D_MODEL), jnp.float32)
    pre_norm_gain = 1.0 + 0.05 * jax.random.normal(ks[1], (DEPTH, D_MODEL), jnp.float32)
    w_in = jax.random.normal(ks[2], (DEPTH, D_MODEL, D_IN), jnp.float32) * D_MODEL ** -0.5
    w_pool = jax.random.normal(ks[3], (DEPTH, POOL_GROUPS, POOL_GROUP, POOL_GROUP), jnp.float32) * POOL_GROUP ** -0.5
    pool_scale = 1.0 + 0.1 * jax.random.normal(ks[4], (DEPTH, D_POOL), jnp.float32)
    w_out = jax.random.normal(ks[5], (DEPTH, D_MIX, D_MODEL), jnp.float32) * D_MIX ** -0.5
    post_norm_gain = 1.0 + 0.05 * jax.random.normal(ks[6], (DEPTH, D_MODEL), jnp.float32)
    return {"x": x, "pre_norm_gain": pre_norm_gain, "w_in": w_in, "w_pool": w_pool,
            "pool_scale": pool_scale, "w_out": w_out, "post_norm_gain": post_norm_gain}

def reference(x, pre_norm_gain, w_in, w_pool, pool_scale, w_out, post_norm_gain):
    b, s, _ = x.shape
    split_at = [D_SB, 2 * D_SB, 3 * D_SB, 4 * D_SB, 4 * D_SB + D_POOL]
    h = x
    for layer in range(DEPTH):
        hn = _rmsnorm(h, pre_norm_gain[layer])
        proj = jnp.einsum('bsd,de->bse', hn, w_in[layer])
        q, k, v, g_a, u_b, g_b = jnp.split(proj, split_at, axis=-1)

        def heads(t):
            return t.reshape(b, s, SB_HEADS, SB_HEAD_DIM).transpose(0, 2, 1, 3)

        y_a = _stick_breaking(heads(q), heads(k), heads(v))
        y_a = y_a.transpose(0, 2, 1, 3).reshape(b, s, D_SB) * jax.nn.silu(g_a)
        y_b = _multiscale_pool(u_b, w_pool[layer], pool_scale[layer]) * jax.nn.silu(g_b)

        mix = jnp.concatenate([y_a, y_b], axis=-1)
        out = jnp.einsum('bse,ed->bsd', mix, w_out[layer])
        h = h + _rmsnorm(out, post_norm_gain[layer])
    return h


_drawn_inputs = setup_inputs


def setup_inputs(seed=0):
    import zlib

    import numpy as np

    out = dict(_drawn_inputs(seed))
    spreads = {}
    factors = {}
    for name, (base, spread) in spreads.items():
        noise = np.random.default_rng([zlib.crc32(name.encode()), seed]).standard_normal(out[name].shape)
        drawn = base * np.exp(spread * noise) if base else spread * noise
        out[name] = __import__('jax').numpy.asarray(drawn.astype(out[name].dtype))
    for name, factor in factors.items():
        out[name] = (out[name] * factor).astype(out[name].dtype)
    return out
```

```python
from contextlib import ExitStack

import concourse.bass as bass
from concourse import mybir

F32 = mybir.dt.float32
F32R = mybir.dt.float32r
ACT = mybir.ActivationFunctionType
ALU = mybir.AluOpType
AX_X = mybir.AxisListType.X

P = 128
BANK = 512
SEQ = 512
D = 2048
KT = D // P
HEADS = 8
HD = 128
D_SB = HEADS * HD
GROUPS = 4
WINDOWS = (2, 4, 8, 16)
MAX_WINDOW = WINDOWS[-1]
TT = SEQ // P
CHUNK = 2048
KC = CHUNK // BANK
KK = KT // KC
V_CHUNKS = (D_SB // BANK) * KK
PER_HEAD = 5
HEAD_CHUNKS = PER_HEAD * HEADS
OUT_CHUNKS = (D // BANK) * KK
SCALE = float(HD) ** -0.5
EPS = 1e-6

WIDTH = [SEQ - P * b for b in range(TT)]
START = [0, BANK, 2 * BANK, BANK + WIDTH[1]]
TRI_COLS = sum(WIDTH)


def hybrid_layer(nc, xT, x, pre_gain, w_v, w_heads, w_pool, pool_scale, w_out, post_gain, out):
    with ExitStack() as ctx:
        def sb(name, shape, dt=F32, scope=ctx):
            return scope.enter_context(nc.sbuf_tensor(name, shape, dt))

        def sem(name):
            return ctx.enter_context(nc.semaphore(name))

        act_hi = sb("act_hi", [P, KT * SEQ], F32R)
        act_lo = sb("act_lo", [P, KT * SEQ], F32R)
        w_hi = [sb(f"w_hi{i}", [P, CHUNK], F32R) for i in range(2)]
        w_lo = [sb(f"w_lo{i}", [P, CHUNK], F32R) for i in range(2)]
        w_raw = [sb(f"w_raw{i}", [P, CHUNK]) for i in range(2)]
        mix = sb("mix", [P, KT * SEQ])
        post_gain_rows = sb("post_gain_rows", [P, D])
        rstd_rows = sb("rstd_rows", [P, SEQ])
        rstd_col = sb("rstd_col", [P, TT])
        ms_col = sb("ms_col", [P, TT])
        neg_half = sb("neg_half", [P, 1])
        ones_col = sb("ones_col", [P, 1])
        pre_gain_col = sb("pre_gain_col", [P, KT])
        pool_scale_col = sb("pool_scale_col", [P, 2 * GROUPS])
        count_fix = sb("count_fix", [P, GROUPS * MAX_WINDOW])
        inv_window = sb("inv_window", [P, GROUPS])
        positions = sb("positions", [P, MAX_WINDOW])
        out_ss = sb("out_ss", [P, TT * 4])
        out_ms = sb("out_ms", [P, TT])
        out_rstd = sb("out_rstd", [P, TT])
        neg_tri = sb("neg_tri", [P, P], F32R)
        neg_ones = sb("neg_ones", [P, P], F32R)

        heads_scope = ExitStack()
        v_rows = sb("v_rows", [P, TT * D_SB], scope=heads_scope)
        q_hi = sb("q_hi", [P, SEQ], F32R, heads_scope)
        q_lo = sb("q_lo", [P, SEQ], F32R, heads_scope)
        k_hi = sb("k_hi", [P, SEQ], F32R, heads_scope)
        k_lo = sb("k_lo", [P, SEQ], F32R, heads_scope)
        tri_hi = sb("tri_hi", [P, TRI_COLS], F32R, heads_scope)
        tri_lo = sb("tri_lo", [P, TRI_COLS], F32R, heads_scope)
        tri = sb("tri", [P, TRI_COLS], scope=heads_scope)
        drained = sb("drained", [P, SEQ], scope=heads_scope)
        work = sb("work", [P, SEQ], scope=heads_scope)
        cumsum = sb("cumsum", [P, MAX_WINDOW + SEQ], scope=heads_scope)
        mixed_hi = sb("mixed_hi", [P, SEQ], F32R, heads_scope)
        mixed_lo = sb("mixed_lo", [P, SEQ], F32R, heads_scope)
        wp_raw = sb("wp_raw", [P, 2 * P], scope=heads_scope)
        heads_scope.close()
        w_hi += [sb(f"w_hi{i}", [P, CHUNK], F32R) for i in (2, 3)]
        w_lo += [sb(f"w_lo{i}", [P, CHUNK], F32R) for i in (2, 3)]

        square = [tri[:, 0:SEQ], tri[:, SEQ:2 * SEQ]]
        ss_part = work
        eye = drained[:, 0:P]
        rstd_diag = cumsum[:, 0:SEQ]
        ones_sq = v_rows[:, TT * D_SB - P:]
        fill = tri[:, 2 * SEQ:2 * SEQ + P]

        ps = ctx.enter_context(nc.psum_tensor("ps", [P, 8 * BANK], F32))

        def bank(i):
            return ps[:, i * BANK:(i + 1) * BANK]

        ROWS = 0
        scores = ps[:, 0:TRI_COLS]
        Y = 3
        ACC = 4
        POOL = 6
        ms_ps = ps[:, POOL * BANK:POOL * BANK + TT]
        rstd_ps = bank(POOL + 1)

        small_loaded = sem("small_loaded")
        rows_gain_loaded = sem("rows_gain_loaded")
        X_PIECES = [(0, 2), (2, 4), (4, 8), (8, 12), (12, 16)]
        x_loaded = [sem(f"x_loaded{i}") for i in range(len(X_PIECES))]
        raw_loaded = [sem(f"raw_loaded{i}") for i in range(2)]
        wp_loaded = sem("wp_loaded")
        out_stored = sem("out_stored")
        w_hi_done = sem("w_hi_done")
        w_split = sem("w_split")
        chunk_done = sem("chunk_done")
        x_hi_done = sem("x_hi_done")
        x_split = sem("x_split")
        squared = sem("squared")
        ss_added = sem("ss_added")
        pool_const = sem("pool_const")
        pool_woken = sem("pool_woken")
        vec_const = sem("vec_const")
        eye_ready = sem("eye_ready")
        ms_summed = sem("ms_summed")
        ms_ready = sem("ms_ready")
        rstd_ready = sem("rstd_ready")
        diag_ready = sem("diag_ready")
        rstd_spread = sem("rstd_spread")
        qk_scaled = sem("qk_scaled")
        qk_hi_done = sem("qk_hi_done")
        qk_ready = sem("qk_ready")
        scores_done = sem("scores_done")
        z_abs = sem("z_abs")
        z_exp = sem("z_exp")
        z_ln = sem("z_ln")
        softplus_done = sem("softplus_done")
        softplus_masked = sem("softplus_masked")
        softplus_hi = sem("softplus_hi")
        softplus_ready = sem("softplus_ready")
        v_hi_done = sem("v_hi_done")
        v_ready = sem("v_ready")
        wp_hi_done = sem("wp_hi_done")
        wp_ready = sem("wp_ready")
        logits_done = sem("logits_done")
        weights_exp = sem("weights_exp")
        weights_masked = sem("weights_masked")
        weights_hi = sem("weights_hi")
        weights_ready = sem("weights_ready")
        y_done = sem("y_done")
        y_free = sem("y_free")
        gate_drained = sem("gate_drained")
        gate_abs = sem("gate_abs")
        gate_exp = sem("gate_exp")
        gate_ln = sem("gate_ln")
        gate_logsig = sem("gate_logsig")
        gate_sig = sem("gate_sig")
        gate_done = sem("gate_done")
        u_drained = sem("u_drained")
        u_summed = sem("u_summed")
        u_window = sem("u_window")
        u_fixed = sem("u_fixed")
        u_mixed = sem("u_mixed")
        mixed_hi_done = sem("mixed_hi_done")
        mixed_ready = sem("mixed_ready")
        pool_done = sem("pool_done")
        pool_free = sem("pool_free")
        mix_hi_done = sem("mix_hi_done")
        mix_split = sem("mix_split")
        rows_done = sem("rows_done")
        rows_free = sem("rows_free")
        rows_squared = sem("rows_squared")
        out_summed = sem("out_summed")
        out_ms_ready = sem("out_ms_ready")
        out_rstd_ready = sem("out_rstd_ready")
        final_done = sem("final_done")

        POOL_CONSTS = 4
        H0 = V_CHUNKS
        O0 = V_CHUNKS + HEAD_CHUNKS
        N_CHUNKS = O0 + OUT_CHUNKS

        def act_tile(t, k):
            return t[:, k * SEQ:(k + 1) * SEQ]

        block = ctx.enter_context(nc.Block())

        @block.sync
        def _(sp):
            for n in range(V_CHUNKS):
                if n >= 2:
                    sp.wait_ge(w_split, n - 1)
                sp.dma_start(w_raw[n % 2][:, :], w_v[n]).then_inc(raw_loaded[n % 2], 16)
                if n == 0:
                    sp.dma_start(pool_scale_col[:, :], pool_scale).then_inc(small_loaded, 16)
                if n == 3:
                    sp.dma_start(post_gain_rows[:, :],
                                 post_gain.partition_broadcast(P)).then_inc(rows_gain_loaded, 16)
            with sp.Fori(0, HEADS // 2) as i:
                for j in range(2):
                    for m in range(PER_HEAD):
                        at = PER_HEAD * j + m
                        n = H0 + 2 * PER_HEAD * i + at
                        sp.wait_ge(w_split, n - 1)
                        sp.dma_start(w_raw[at % 2][:, :],
                                     w_heads[2 * PER_HEAD * i + at]).then_inc(raw_loaded[at % 2], 16)
                        if m == 1:
                            sp.wait_ge(wp_ready, 2 * i + j + 1)
                            sp.dma_start(wp_raw[:, :], w_pool[2 * i + j]).then_inc(wp_loaded, 16)
            with sp.Fori(0, OUT_CHUNKS // 4) as dc:
                for kk in range(4):
                    sp.wait_ge(w_split, O0 + 4 * dc + kk - 1)
                    sp.dma_start(w_raw[kk % 2][:, :], w_out[4 * dc + kk]).then_inc(raw_loaded[kk % 2], 16)
            for s in range(2):
                sp.wait_ge(w_split, N_CHUNKS - 1 + s)
                sp.dma_start(w_raw[s][:, :], x[s]).then_inc(raw_loaded[s], 16)
            for s in range(TT):
                for half in range(2):
                    sp.wait_ge(final_done, 2 * s + half + 1)
                    a = half * D // 2
                    sp.dma_start(out[s][:, a:a + D // 2],
                                 mix[:, s * D + a:s * D + a + D // 2]).then_inc(out_stored, 16)
                if s + 2 < TT:
                    sp.dma_start(w_raw[s % 2][:, :], x[s + 2]).then_inc(raw_loaded[s % 2], 16)
            sp.wait_ge(out_stored, 16 * 2 * TT)

        @block.scalar
        def _(act):
            act.dma_start(pre_gain_col[:, :], pre_gain).then_inc(small_loaded, 16)
            for i, (a, b) in enumerate(X_PIECES):
                act.dma_start(mix[:, a * SEQ:b * SEQ], xT[:, a * SEQ:b * SEQ]).then_inc(x_loaded[i], 16)
            act.preload_act_table_set("natural_log_exp_and_others")

            def w_hi_of(n, raw, slot, count):
                act.wait_ge(raw_loaded[raw], 16 * count)
                act.activation(w_hi[slot][:, :], w_raw[raw][:, :], ACT.Copy).then_inc(w_hi_done, 1)

            def x_hi_of(piece):
                act.wait_ge(x_loaded[piece], 16)
                for k in range(*X_PIECES[piece]):
                    act.activation(act_tile(act_hi, k), act_tile(mix, k), ACT.Copy,
                                   scale=pre_gain_col[:, k:k + 1]).then_inc(x_hi_done, 1)

            def square_of(k):
                if k >= 3:
                    act.wait_ge(ss_added, k - 2)
                dst = ss_part[:, :] if k == 0 else square[k % 2]
                act.activation(dst, act_tile(mix, k), ACT.Square).then_inc(squared, 1)

            act.wait_ge(small_loaded, 32)
            x_hi_of(0)
            w_hi_of(0, 0, 0, 1)
            x_hi_of(1)
            x_hi_of(2)
            w_hi_of(1, 1, 1, 1)
            x_hi_of(3)
            x_hi_of(4)
            for k in range(KT // 2):
                square_of(k)
            for n in range(V_CHUNKS):
                act.wait_ge(chunk_done, n + 1)
                w_hi_of(n + 2, n % 2, n % 2, (n + 2) // 2 + 1)
                if n == 0:
                    for k in range(KT // 2, KT):
                        square_of(k)

            def gate(h, which):
                n = 2 * h + which + 1
                act.wait_ge(gate_drained, n + 1)
                act.activation(work[:, :], drained[:, :], ACT.Abs).then_inc(gate_abs, 1)
                act.wait_ge(gate_abs, n)
                act.activation(work[:, :], work[:, :], ACT.Exp, scale=-1.0).then_inc(gate_exp, 1)
                act.wait_ge(gate_exp, n)
                act.activation(work[:, :], work[:, :], ACT.Ln, bias=1.0).then_inc(gate_ln, 1)
                act.wait_ge(gate_logsig, n)
                act.activation(work[:, :], work[:, :], ACT.Exp).then_inc(gate_sig, 1)

            with act.Fori(0, HEADS // 2) as i:
                for j in range(2):
                    h = 2 * i + j
                    for m in range(PER_HEAD):
                        at = PER_HEAD * j + m
                        n = H0 + 2 * PER_HEAD * i + at
                        act.wait_ge(chunk_done, n + 1)
                        w_hi_of(n + 2, at % 2, at % 2, PER_HEAD * i + (H0 + at + 2) // 2 + 1)
                        if m == 1:
                            act.wait_ge(scores_done, h + 1)
                            act.activation(tri[:, :], scores, ACT.Abs).then_inc(z_abs, 1)
                            act.wait_ge(z_abs, h + 1)
                            act.activation(tri[:, :], tri[:, :], ACT.Exp, scale=-1.0).then_inc(z_exp, 1)
                            act.wait_ge(z_exp, h + 1)
                            act.activation(tri[:, :], tri[:, :], ACT.Ln, bias=1.0).then_inc(z_ln, 1)
                        if m == 2:
                            act.wait_ge(softplus_masked, 2 * h + 2)
                            act.activation(tri_hi[:, :], tri[:, :], ACT.Copy).then_inc(softplus_hi, 1)
                            gate(h, 0)
                        if m == 3:
                            act.wait_ge(logits_done, h + 1)
                            act.activation(tri[:, :], scores, ACT.Exp).then_inc(weights_exp, 1)
                            act.wait_ge(weights_masked, 2 * h + 2)
                            act.activation(tri_hi[:, :], tri[:, :], ACT.Copy).then_inc(weights_hi, 1)
                        if m == 4:
                            gate(h, 1)

            act.wait_ge(gate_done, 1 + 2 * HEADS)
            for k in range(KT):
                if k == KT - 2:
                    act.wait_ge(pool_free, 1 + 2 * GROUPS)
                act.activation(act_tile(act_hi, k), act_tile(mix, k), ACT.Copy).then_inc(mix_hi_done, 1)

            def rows_square(s, dc):
                act.activation(bank(ACC + s), bank(ROWS + s), ACT.Square,
                               accum_out=out_ss[:, bass.ds(4 * s + dc, 1)]).then_inc(rows_squared, 1)

            with act.Fori(0, 3) as dc:
                for kk in range(KK):
                    n = O0 + KK * dc + kk
                    if kk == 3:
                        for s in range(TT - 1):
                            act.wait_ge(rows_done, 3 * (2 + dc) + s + 1)
                            rows_square(s, dc)
                    act.wait_ge(chunk_done, n + 1)
                    w_hi_of(n + 2, kk % 2, kk % 2, 2 * dc + (O0 + kk + 2) // 2 + 1)
                rows_square(TT - 1, dc)
            for i in (2, 3):
                n = N_CHUNKS - 4 + i
                w_hi_of(n, i % 2, i, n // 2 + 1)
            for s in range(TT):
                act.wait_ge(rows_done, 3 * 5 + s + 1)
                rows_square(s, 3)

        @block.vector
        def _(dve):
            for free in (u_drained, gate_drained, gate_done, y_free, pool_free, wp_ready):
                dve.sem_inc(free, 1)
            dve.memset(neg_half[:, :], -0.5).then_inc(vec_const, 1)
            dve.memset(ones_col[:, :], 1.0).then_inc(vec_const, 1)
            dve.memset(ones_sq, 1.0).then_inc(vec_const, 1)
            for g, w in enumerate(WINDOWS):
                dve.memset(inv_window[:, g:g + 1], 1.0 / w).then_inc(vec_const, 1)
            VEC = 3 + GROUPS

            def w_lo_of(n, raw, slot):
                dve.wait_ge(w_hi_done, n + 1)
                dve.tensor_tensor(w_lo[slot][:, :], w_raw[raw][:, :], w_hi[slot][:, :].bitcast(F32),
                                  ALU.subtract).then_inc(w_split, 1)

            def x_lo_of(piece):
                for k in range(*X_PIECES[piece]):
                    dve.wait_ge(x_hi_done, k + 1)
                    dve.scalar_tensor_tensor(act_tile(act_lo, k), act_tile(mix, k),
                                             pre_gain_col[:, k:k + 1],
                                             act_tile(act_hi, k).bitcast(F32),
                                             ALU.mult, ALU.subtract).then_inc(x_split, 1)

            def add_square(k):
                dve.wait_ge(squared, k + 1)
                if k >= 2:
                    dve.wait_ge(ss_added, k - 1)
                dve.tensor_tensor(ss_part[:, :], ss_part[:, :], square[k % 2],
                                  ALU.add).then_inc(ss_added, 1)

            dve.wait_ge(small_loaded, 32)
            x_lo_of(0)
            w_lo_of(0, 0, 0)
            x_lo_of(1)
            x_lo_of(2)
            w_lo_of(1, 1, 1)
            x_lo_of(3)
            x_lo_of(4)
            for k in range(1, KT // 2):
                add_square(k)
            dve.wait_ge(pool_const, 1)
            dve.reciprocal(positions[:, :], positions[:, :]).then_inc(vec_const, 1)
            dve.wait_ge(vec_const, VEC + 1)
            for g, w in enumerate(WINDOWS):
                dve.tensor_scalar(count_fix[:, g * MAX_WINDOW:(g + 1) * MAX_WINDOW], positions[:, :],
                                  float(w), 1.0, ALU.mult, ALU.max).then_inc(vec_const, 1)

            def v_rows_of(g, s):
                if s < TT - 1:
                    dve.wait_ge(rows_done, 3 * g + s + 1)
                else:
                    dve.wait_ge(chunk_done, KK * (g + 1))
                ins = dve.tensor_scalar(v_rows[:, s * D_SB + g * BANK:s * D_SB + (g + 1) * BANK],
                                        bank(ROWS + s), rstd_col[:, s:s + 1], None, ALU.mult)
                ins.then_inc(rows_free, 1)

            for n in range(V_CHUNKS):
                w_lo_of(n + 2, n % 2, n % 2)
                if n == 0:
                    for k in range(KT // 2, KT):
                        add_square(k)
                if n == 2:
                    dve.wait_ge(ms_summed, 1)
                    dve.tensor_scalar(ms_col[:, :], ms_ps, 1.0 / D, EPS, ALU.mult,
                                      ALU.add).then_inc(ms_ready, 1)
                    dve.wait_ge(rstd_ready, 1)
                    dve.wait_ge(eye_ready, 2)
                    for s in range(TT):
                        dve.tensor_scalar(rstd_diag[:, s * P:(s + 1) * P], eye, rstd_col[:, s:s + 1],
                                          None, ALU.mult).then_inc(diag_ready, 1)
                    for s in range(TT):
                        v_rows_of(0, s)
                if n == 3:
                    dve.wait_ge(rstd_spread, 1)
                    dve.tensor_copy(rstd_rows[:, :], rstd_ps).then_inc(rstd_ready, 1)
                    dve.memset(cumsum[:, 0:MAX_WINDOW], 0.0).then_inc(vec_const, 1)
                if n == V_CHUNKS - 2:
                    for s in range(TT):
                        v_rows_of(1, s)
            dve.wait_ge(rstd_ready, 2)
            dve.wait_ge(rows_free, 2 * TT)
            dve.wait_ge(vec_const, VEC + 2 + GROUPS)

            def drain_qk(at, n, count, hi, lo, scale):
                dve.wait_ge(chunk_done, n + 1)
                if hi is q_hi:
                    dve.wait_ge(gate_done, count)
                else:
                    dve.wait_ge(qk_ready, count - 1)
                dve.scalar_tensor_tensor(drained[:, :], bank(ACC + at % 2), scale, rstd_rows[:, :],
                                         ALU.mult, ALU.mult).then_inc(qk_scaled, 1)
                dve.wait_ge(qk_scaled, count)
                dve.tensor_copy(hi[:, :], drained[:, :]).then_inc(qk_hi_done, 1)
                dve.wait_ge(qk_hi_done, count)
                dve.tensor_tensor(lo[:, :], drained[:, :], hi[:, :].bitcast(F32),
                                  ALU.subtract).then_inc(qk_ready, 1)

            def drain_gate(at, n):
                dve.wait_ge(chunk_done, n + 1)
                dve.tensor_tensor(drained[:, :], bank(ACC + at % 2), rstd_rows[:, :],
                                  ALU.mult).then_inc(gate_drained, 1)

            def gate(h, which, tile):
                n = 2 * h + which + 1
                dve.wait_ge(gate_ln, n)
                dve.scalar_tensor_tensor(work[:, :], drained[:, :], 0.0, work[:, :],
                                         ALU.min, ALU.subtract).then_inc(gate_logsig, 1)
                dve.wait_ge(gate_sig, n)
                dve.tensor_tensor(mix[:, bass.ds(tile * SEQ, SEQ)], drained[:, :], work[:, :],
                                  ALU.mult).then_inc(gate_done, 1)

            with dve.Fori(0, HEADS // 2) as i:
                lagged = dve.snap(dve.to_reg(MAX_WINDOW - (2 << i)), min_val=0, max_val=MAX_WINDOW - 2)
                for j in range(2):
                    h = 2 * i + j
                    at = PER_HEAD * j
                    n = H0 + 2 * PER_HEAD * i + at
                    drain_qk(at, n, 2 * h + 1, q_hi, q_lo, SCALE)
                    w_lo_of(n + 2, at % 2, at % 2)
                    at, n = at + 1, n + 1
                    drain_qk(at, n, 2 * h + 2, k_hi, k_lo, 1.0)
                    w_lo_of(n + 2, at % 2, at % 2)
                    dve.wait_ge(z_ln, h + 1)
                    dve.scalar_tensor_tensor(tri[:, :], scores, 0.0, tri[:, :],
                                             ALU.max, ALU.add).then_inc(softplus_done, 1)
                    at, n = at + 1, n + 1
                    drain_gate(at, n)
                    w_lo_of(n + 2, at % 2, at % 2)
                    dve.wait_ge(softplus_hi, h + 1)
                    dve.tensor_tensor(tri_lo[:, :], tri[:, :], tri_hi[:, :].bitcast(F32),
                                      ALU.subtract).then_inc(softplus_ready, 1)
                    dve.wait_ge(v_hi_done, h + 1)
                    dve.tensor_tensor(q_lo[:, :].rearrange("p (b d) -> p b d", b=TT),
                                      v_rows[:, :].rearrange("p (b c) -> p b c", b=TT)
                                      [:, :, bass.ds(h * HD, HD)],
                                      q_hi[:, :].rearrange("p (b d) -> p b d", b=TT).bitcast(F32),
                                      ALU.subtract).then_inc(v_ready, 1)
                    dve.wait_ge(wp_hi_done, h + 1)
                    dve.tensor_tensor(k_lo[:, 0:2 * P], wp_raw[:, :], k_hi[:, 0:2 * P].bitcast(F32),
                                      ALU.subtract).then_inc(wp_ready, 1)
                    gate(h, 0, h)
                    at, n = at + 1, n + 1
                    dve.wait_ge(chunk_done, n + 1)
                    dve.wait_ge(gate_done, 2 * h + 2)
                    dve.tensor_tensor(drained[:, :], bank(ACC + at % 2), rstd_rows[:, :],
                                      ALU.mult).then_inc(u_drained, 1)
                    dve.wait_ge(u_drained, h + 2)
                    dve.tensor_tensor_scan(cumsum[:, MAX_WINDOW:], ones_col[:, 0:1].to_broadcast([P, SEQ]),
                                           drained[:, :], 0.0, ALU.mult, ALU.add).then_inc(u_summed, 1)
                    w_lo_of(n + 2, at % 2, at % 2)
                    dve.wait_ge(u_summed, h + 1)
                    dve.tensor_tensor(work[:, :], cumsum[:, MAX_WINDOW:],
                                      cumsum[:, bass.ds(lagged, SEQ)],
                                      ALU.subtract).then_inc(u_window, 1)
                    dve.wait_ge(u_window, h + 1)
                    dve.tensor_tensor(work[:, 0:MAX_WINDOW], work[:, 0:MAX_WINDOW],
                                      count_fix[:, bass.ds(i * MAX_WINDOW, MAX_WINDOW)],
                                      ALU.mult).then_inc(u_fixed, 1)
                    dve.wait_ge(u_fixed, h + 1)
                    dve.scalar_tensor_tensor(work[:, :], work[:, :], inv_window[:, bass.ds(i, 1)],
                                             drained[:, :], ALU.mult, ALU.subtract).then_inc(u_mixed, 1)
                    dve.wait_ge(u_mixed, h + 1)
                    dve.tensor_copy(mixed_hi[:, :], work[:, :]).then_inc(mixed_hi_done, 1)
                    dve.wait_ge(mixed_hi_done, h + 1)
                    dve.tensor_tensor(mixed_lo[:, :], work[:, :], mixed_hi[:, :].bitcast(F32),
                                      ALU.subtract).then_inc(mixed_ready, 1)
                    dve.wait_ge(weights_hi, h + 1)
                    dve.tensor_tensor(tri_lo[:, :], tri[:, :], tri_hi[:, :].bitcast(F32),
                                      ALU.subtract).then_inc(weights_ready, 1)
                    at, n = at + 1, n + 1
                    dve.wait_ge(mixed_ready, h + 1)
                    drain_gate(at, n)
                    w_lo_of(n + 2, at % 2, at % 2)
                    dve.wait_ge(y_done, h + 1)
                    dve.tensor_tensor(mix[:, bass.ds(h * SEQ, SEQ)], bank(Y),
                                      mix[:, bass.ds(h * SEQ, SEQ)], ALU.mult).then_inc(y_free, 1)
                    gate(h, 1, HEADS + h)
                    if j == 1:
                        dve.wait_ge(pool_done, i + 1)
                        dve.wait_ge(gate_done, 2 * h + 3)
                        for t in range(2):
                            rows = mix[:, bass.ds((HEADS + 2 * i + t) * SEQ, SEQ)]
                            dve.scalar_tensor_tensor(rows, bank(POOL + t),
                                                     pool_scale_col[:, bass.ds(2 * i + t, 1)], rows,
                                                     ALU.mult, ALU.mult).then_inc(pool_free, 1)

            for k in range(KT):
                dve.wait_ge(mix_hi_done, k + 1)
                dve.tensor_tensor(act_tile(act_lo, k), act_tile(mix, k),
                                  act_tile(act_hi, k).bitcast(F32),
                                  ALU.subtract).then_inc(mix_split, 1)

            def rows_gain(s, dc):
                dve.tensor_tensor(mix[:, bass.ds(s * D + dc * BANK, BANK)], bank(ROWS + s),
                                  post_gain_rows[:, bass.ds(dc * BANK, BANK)],
                                  ALU.mult).then_inc(rows_free, 1)

            dve.wait_ge(rows_gain_loaded, 16)
            dve.wait_ge(mix_split, KT)
            with dve.Fori(0, 3) as dc:
                for kk in range(KK):
                    n = O0 + KK * dc + kk
                    if kk == 3:
                        for s in range(TT - 1):
                            dve.wait_ge(rows_squared, 4 * dc + s + 1)
                            rows_gain(s, dc)
                    w_lo_of(n + 2, kk % 2, kk % 2)
                dve.wait_ge(rows_squared, 4 * dc + TT)
                rows_gain(TT - 1, dc)
            for i in (2, 3):
                w_lo_of(N_CHUNKS - 4 + i, i % 2, i)
            for s in range(TT):
                dve.wait_ge(rows_squared, 12 + s + 1)
                rows_gain(s, 3)
                dve.tensor_reduce(out_ms[:, s:s + 1], out_ss[:, 4 * s:4 * s + 4], AX_X,
                                  ALU.add).then_inc(out_summed, 1)
                dve.wait_ge(out_summed, s + 1)
                dve.tensor_scalar(out_ms[:, s:s + 1], out_ms[:, s:s + 1], 1.0 / D, EPS,
                                  ALU.mult, ALU.add).then_inc(out_ms_ready, 1)
                dve.wait_ge(out_rstd_ready, s + 1)
                dve.wait_ge(raw_loaded[s % 2], 16 * (N_CHUNKS // 2 + s // 2 + 1))
                dve.wait_ge(rows_free, 2 * TT + 12 + s + 1)
                for half in range(2):
                    rows = mix[:, s * D + half * D // 2:s * D + (half + 1) * D // 2]
                    dve.scalar_tensor_tensor(rows, rows, out_rstd[:, s:s + 1],
                                             w_raw[s % 2][:, half * D // 2:(half + 1) * D // 2],
                                             ALU.mult, ALU.add).then_inc(final_done, 1)

        @block.gpsimd
        def _(pool):
            pool.iota(positions[:, :], [[1, MAX_WINDOW]], base=1, channel_multiplier=0,
                      allow_small_or_imprecise_dtypes=True).then_inc(pool_const, 1)
            pool.memset(eye, 0.0).then_inc(eye_ready, 1)
            pool.wait_ge(eye_ready, 1)
            pool.affine_select(out=eye, in_=eye, compare_op=ALU.not_equal, fill=1.0, base=0,
                               pattern=[[-1, P]], channel_multiplier=1).then_inc(eye_ready, 1)
            pool.memset(fill, -1.0).then_inc(pool_const, 1)
            pool.wait_ge(pool_const, 2)
            pool.tensor_copy(neg_ones[:, :], fill).then_inc(pool_const, 1)
            pool.affine_select(out=neg_tri[:, :], in_=fill, compare_op=ALU.is_ge, fill=0.0, base=0,
                               pattern=[[-1, P]], channel_multiplier=1).then_inc(pool_const, 1)
            pool.wait_ge(ms_ready, 1)
            pool.wait_ge(vec_const, 1)
            pool.tensor_tensor(rstd_col[:, :], ms_col[:, :], neg_half[:, 0:1].to_broadcast([P, TT]),
                               ALU.pow).then_inc(rstd_ready, 1)

            def mask(done):
                for first, step in ((START[0], START[1] - START[0]), (START[3], START[2] - START[3])):
                    sq = tri[:, first:first + 2 * step].rearrange("p (b c) -> p b c", b=2)[:, :, 0:P]
                    pool.affine_select(out=sq, in_=sq, compare_op=ALU.is_gt, fill=0.0, base=0,
                                       pattern=[[0, 2], [1, P]], channel_multiplier=-1).then_inc(done, 1)

            with pool.Fori(0, HEADS // 2) as i:
                for j in range(2):
                    h = 2 * i + j
                    pool.wait_ge(scores_done, h + 1)
                    pool.tensor_copy(q_hi[:, :].rearrange("p (b d) -> p b d", b=TT),
                                     v_rows[:, :].rearrange("p (b c) -> p b c", b=TT)
                                     [:, :, bass.ds(h * HD, HD)]).then_inc(v_hi_done, 1)
                    pool.wait_ge(wp_loaded, 16 * (h + 1)).then_inc(pool_woken, 1)
                    pool.tensor_copy(k_hi[:, 0:2 * P], wp_raw[:, :]).then_inc(wp_hi_done, 1)
                    pool.wait_ge(softplus_done, h + 1).then_inc(pool_woken, 1)
                    mask(softplus_masked)
                    pool.wait_ge(weights_exp, h + 1).then_inc(pool_woken, 1)
                    mask(weights_masked)

            for s in range(TT):
                pool.wait_ge(out_ms_ready, s + 1)
                pool.tensor_tensor(out_rstd[:, s:s + 1], out_ms[:, s:s + 1], neg_half[:, 0:1],
                                   ALU.pow).then_inc(out_rstd_ready, 1)

        @block.tensor
        def _(pe):
            def three(dst, sta, mov, first, last):
                pe.matmul(dst, sta[0], mov[0], start=first, stop=False, skip_group_check=True)
                pe.matmul(dst, sta[0], mov[1], start=False, stop=False, skip_group_check=True)
                return pe.matmul(dst, sta[1], mov[0], start=False, stop=last, skip_group_check=True)

            def both(pair, a, b):
                return pair[0][:, a:b], pair[1][:, a:b]

            acts = (act_hi, act_lo)
            ws = list(zip(w_hi, w_lo))

            def rows_tile(s, kk, slot):
                for k in range(KC):
                    a = (kk * KC + k) * SEQ + s * P
                    mm = three(bank(ROWS + s), both(acts, a, a + P),
                               both(ws[slot], k * BANK, (k + 1) * BANK),
                               kk == 0 and k == 0, kk == KK - 1 and k == KC - 1)
                return mm

            for g in range(2):
                for kk in range(KK):
                    n = KK * g + kk
                    pe.wait_ge(w_split, n + 1)
                    if g == 0:
                        pe.wait_ge(x_split, KC * (kk + 1))
                    for s in range(TT):
                        if kk == 0 and g == 1:
                            pe.wait_ge(rows_free, s + 1)
                        mm = rows_tile(s, kk, n % 2)
                        if kk == KK - 1 and s < TT - 1:
                            mm.then_inc(rows_done, 1)
                    mm.then_inc(chunk_done, 1)
                    if n == 2:
                        pe.wait_ge(ss_added, KT - 1)
                        pe.wait_ge(vec_const, 3)
                        for s in range(TT):
                            mm = pe.matmul(ms_ps[:, s:s + 1], ss_part[:, s * P:(s + 1) * P],
                                           ones_col[:, 0:1], start=True, stop=True)
                        mm.then_inc(ms_summed, 1)
                    if n == 3:
                        pe.wait_ge(diag_ready, TT)
                        pe.matmul(rstd_ps, ones_sq, rstd_diag, start=True,
                                  stop=True).then_inc(rstd_spread, 1)

            def column_tiles(at, k0, k1):
                for k in range(k0, k1):
                    mm = three(bank(ACC + at % 2), both(ws[at % 2], k * P, (k + 1) * P),
                               both(acts, k * SEQ, (k + 1) * SEQ), k == 0, k == KT - 1)
                return mm

            def tri_part(b, skip=0):
                return START[b] + skip * P, START[b] + WIDTH[b]

            def qk(h):
                pe.wait_ge(qk_ready, 2 * h + 2)
                for b in range(TT):
                    a, z = tri_part(b)
                    mm = three(ps[:, a:z], both((k_hi, k_lo), b * P, (b + 1) * P),
                               both((q_hi, q_lo), b * P, SEQ), b < 3, False)
                mm.then_inc(scores_done, 1)

            def suffix_sums(h):
                pe.wait_ge(softplus_ready, h + 1)
                for b in range(TT):
                    for later in range(b, TT):
                        a, z = tri_part(b, later - b)
                        src, end = tri_part(later)
                        sta = neg_tri if later == b else neg_ones
                        pe.matmul(ps[:, a:z], sta[:, :], tri_hi[:, src:end], start=False,
                                  stop=False, skip_group_check=True)
                        mm = pe.matmul(ps[:, a:z], sta[:, :], tri_lo[:, src:end], start=False,
                                       stop=later == TT - 1, skip_group_check=True)
                mm.then_inc(logits_done, 1)

            def weighted_values(h):
                pe.wait_ge(weights_ready, h + 1)
                pe.wait_ge(v_ready, h + 1)
                pe.wait_ge(y_free, h + 1)
                for b in range(TT):
                    a, z = tri_part(b)
                    mm = three(bank(Y)[:, b * P:], both((q_hi, q_lo), b * P, (b + 1) * P),
                               both((tri_hi, tri_lo), a, z), b == 0, b == TT - 1)
                mm.then_inc(y_done, 1)

            def pool_tiles(i, j):
                pe.wait_ge(mixed_ready, 2 * i + j + 1)
                pe.wait_ge(wp_ready, 2 * i + j + 2)
                if j == 0:
                    pe.wait_ge(pool_free, 2 * i + 1)
                for t in range(2):
                    mm = three(bank(POOL + t), both((k_hi, k_lo), t * P, (t + 1) * P),
                               both((mixed_hi, mixed_lo), 0, SEQ), j == 0, j == 1)
                if j == 1:
                    mm.then_inc(pool_done, 1)

            pe.wait_ge(pool_const, POOL_CONSTS)
            with pe.Fori(0, HEADS // 2) as i:
                for j in range(2):
                    h = 2 * i + j
                    for m in range(PER_HEAD):
                        at = PER_HEAD * j + m
                        n = H0 + 2 * PER_HEAD * i + at
                        pe.wait_ge(w_split, n + 1)
                        if m == 0:
                            pe.wait_ge(u_drained, h + 1)
                        if m == 1:
                            pe.wait_ge(gate_drained, 2 * h + 1)
                        if m == 2:
                            pe.wait_ge(qk_scaled, 2 * h + 1)
                        if m == 3:
                            pe.wait_ge(qk_scaled, 2 * h + 2)
                        if m == 4:
                            pe.wait_ge(gate_drained, 2 * h + 2)
                        if m == 2:
                            column_tiles(at, 0, KT // 2)
                            qk(h)
                            column_tiles(at, KT // 2, KT).then_inc(chunk_done, 1)
                        else:
                            column_tiles(at, 0, KT).then_inc(chunk_done, 1)
                        if m == 3:
                            suffix_sums(h)
                    weighted_values(h)
                    pool_tiles(i, j)

            with pe.Fori(0, 3) as dc:
                for kk in range(KK):
                    n = O0 + KK * dc + kk
                    pe.wait_ge(w_split, n + 1)
                    pe.wait_ge(mix_split, KC * (kk + 1))
                    for s in range(TT):
                        if kk == 0:
                            pe.wait_ge(rows_free, 4 * dc + s + 5)
                        mm = rows_tile(s, kk, kk % 2)
                        if kk == KK - 1 and s < TT - 1:
                            mm.then_inc(rows_done, 1)
                    mm.then_inc(chunk_done, 1)
            for s in range(TT):
                pe.wait_ge(rows_free, 4 * 3 + s + 5)
                for kk in range(KK):
                    if s == 0:
                        pe.wait_ge(w_split, N_CHUNKS - KK + kk + 1)
                    mm = rows_tile(s, kk, kk)
                mm.then_inc(rows_done, 1)


def kernel(x, pre_norm_gain, w_in, w_pool, pool_scale, w_out, post_norm_gain):
    import numpy as np
    import concourse.bacc as bacc
    from concourse.bass_utils import run_bass_kernel_spmd

    x, w_in, w_out = np.asarray(x)[0], np.asarray(w_in)[0], np.asarray(w_out)[0]
    w_pool = np.asarray(w_pool)[0]

    def features_first(a):
        return a.reshape(-1, P, a.shape[-1]).transpose(1, 0, 2)

    def moving(w):
        c = w.reshape(KT // KC, KC, P, -1, BANK).transpose(3, 0, 2, 1, 4)
        return c.reshape(-1, P, CHUNK)

    parts = w_in.reshape(KT, P, 6, HEADS, P).transpose(3, 2, 1, 0, 4)
    heads = parts[:, [0, 1, 3, 4, 5]].reshape(HEAD_CHUNKS, P, CHUNK)
    arrays = {
        "xT": features_first(x.T).reshape(P, KT * SEQ),
        "x": x.reshape(TT, P, D),
        "pre_gain": np.asarray(pre_norm_gain).reshape(KT, P).T,
        "w_v": moving(w_in[:, 2 * D_SB:3 * D_SB]),
        "w_heads": heads,
        "w_pool": w_pool.reshape(2 * GROUPS, P, 2 * P),
        "pool_scale": np.asarray(pool_scale).reshape(2 * GROUPS, P).T,
        "w_out": moving(w_out),
        "post_gain": np.asarray(post_norm_gain).reshape(D),
    }
    arrays = {name: np.ascontiguousarray(a) for name, a in arrays.items()}
    nc = bacc.Bacc("TRN2", target_bir_lowering=False, num_devices=1)
    args = {name: nc.dram_tensor(name, a.shape, F32, kind="ExternalInput").ap()
            for name, a in arrays.items()}
    out = nc.dram_tensor("out", (TT, P, D), F32, kind="ExternalOutput").ap()
    hybrid_layer(nc, out=out, **args)
    result = run_bass_kernel_spmd(nc, [arrays], core_ids=[0])
    return result.results[0]["out"].reshape(1, SEQ, D)
```

```python
from contextlib import ExitStack

import concourse.bass as bass
from concourse import mybir

F32 = mybir.dt.float32
F32R = mybir.dt.float32r
ACT = mybir.ActivationFunctionType
ALU = mybir.AluOpType
AX_X = mybir.AxisListType.X

P = 128
BANK = 512
SEQ = 512
D = 2048
KT = D // P
HEADS = 8
HD = 128
D_SB = HEADS * HD
GROUPS = 4
WINDOWS = (2, 4, 8, 16)
MAX_WINDOW = WINDOWS[-1]
TT = SEQ // P
CHUNK = 2048
KC = CHUNK // BANK
KK = KT // KC
V_CHUNKS = (D_SB // BANK) * KK
PER_HEAD = 5
HEAD_CHUNKS = PER_HEAD * HEADS
OUT_CHUNKS = (D // BANK) * KK
SCALE = float(HD) ** -0.5
EPS = 1e-6

WIDTH = [SEQ - P * b for b in range(TT)]
START = [0, BANK, 2 * BANK, BANK + WIDTH[1]]
TRI_COLS = sum(WIDTH)


def hybrid_layer(nc, xT, x, pre_gain, w_v, w_heads, w_pool, pool_scale, w_out, post_gain, out):
    with ExitStack() as ctx:
        def sb(name, shape, dt=F32, scope=ctx):
            return scope.enter_context(nc.sbuf_tensor(name, shape, dt))

        def sem(name):
            return ctx.enter_context(nc.semaphore(name))

        act_hi = sb("act_hi", [P, KT * SEQ], F32R)
        act_lo = sb("act_lo", [P, KT * SEQ], F32R)
        w_hi = [sb(f"w_hi{i}", [P, CHUNK], F32R) for i in range(2)]
        w_lo = [sb(f"w_lo{i}", [P, CHUNK], F32R) for i in range(2)]
        w_raw = [sb(f"w_raw{i}", [P, CHUNK]) for i in range(2)]
        mix = sb("mix", [P, KT * SEQ])
        post_gain_rows = sb("post_gain_rows", [P, D])
        rstd_rows = sb("rstd_rows", [P, SEQ])
        rstd_col = sb("rstd_col", [P, TT])
        ms_col = sb("ms_col", [P, TT])
        neg_half = sb("neg_half", [P, 1])
        ones_col = sb("ones_col", [P, 1])
        pre_gain_col = sb("pre_gain_col", [P, KT])
        pool_scale_col = sb("pool_scale_col", [P, 2 * GROUPS])
        count_fix = sb("count_fix", [P, GROUPS * MAX_WINDOW])
        inv_window = sb("inv_window", [P, GROUPS])
        positions = sb("positions", [P, MAX_WINDOW])
        out_ss = sb("out_ss", [P, TT * 4])
        out_ms = sb("out_ms", [P, TT])
        out_rstd = sb("out_rstd", [P, TT])
        neg_tri = sb("neg_tri", [P, P], F32R)
        neg_ones = sb("neg_ones", [P, P], F32R)

        heads_scope = ExitStack()
        v_rows = sb("v_rows", [P, TT * D_SB], scope=heads_scope)
        q_hi = sb("q_hi", [P, SEQ], F32R, heads_scope)
        q_lo = sb("q_lo", [P, SEQ], F32R, heads_scope)
        k_hi = sb("k_hi", [P, SEQ], F32R, heads_scope)
        k_lo = sb("k_lo", [P, SEQ], F32R, heads_scope)
        tri_hi = sb("tri_hi", [P, TRI_COLS], F32R, heads_scope)
        tri_lo = sb("tri_lo", [P, TRI_COLS], F32R, heads_scope)
        tri = sb("tri", [P, TRI_COLS], scope=heads_scope)
        drained = sb("drained", [P, SEQ], scope=heads_scope)
        work = sb("work", [P, SEQ], scope=heads_scope)
        cumsum = sb("cumsum", [P, MAX_WINDOW + SEQ], scope=heads_scope)
        mixed_hi = sb("mixed_hi", [P, SEQ], F32R, heads_scope)
        mixed_lo = sb("mixed_lo", [P, SEQ], F32R, heads_scope)
        wp_raw = sb("wp_raw", [P, 2 * P], scope=heads_scope)
        heads_scope.close()
        w_hi += [sb(f"w_hi{i}", [P, CHUNK], F32R) for i in (2, 3)]
        w_lo += [sb(f"w_lo{i}", [P, CHUNK], F32R) for i in (2, 3)]

        square = [tri[:, 0:SEQ], tri[:, SEQ:2 * SEQ]]
        ss_part = work
        eye = drained[:, 0:P]
        rstd_diag = cumsum[:, 0:SEQ]
        ones_sq = v_rows[:, TT * D_SB - P:]
        fill = tri[:, 2 * SEQ:2 * SEQ + P]

        ps = ctx.enter_context(nc.psum_tensor("ps", [P, 8 * BANK], F32))

        def bank(i):
            return ps[:, i * BANK:(i + 1) * BANK]

        ROWS = 0
        scores = ps[:, 0:TRI_COLS]
        Y = 3
        ACC = 4
        POOL = 6
        ms_ps = ps[:, POOL * BANK:POOL * BANK + TT]
        rstd_ps = bank(POOL + 1)

        gain_loaded = sem("gain_loaded")
        scale_loaded = sem("scale_loaded")
        rows_gain_loaded = sem("rows_gain_loaded")
        X_PIECES = [(0, 1), (1, 2), (2, 4), (4, 8), (8, 12), (12, 16)]
        W0_PIECES = [(0, 1), (1, 2), (2, 4)]
        x_loaded = [sem(f"x_loaded{i}") for i in range(len(X_PIECES))]
        raw_loaded = [sem(f"raw_loaded{i}") for i in range(2)]
        w0_loaded = [sem(f"w0_loaded{i}") for i in range(len(W0_PIECES))]
        w0_hi_done = sem("w0_hi_done")
        w0_split = sem("w0_split")
        wp_loaded = sem("wp_loaded")
        out_stored = sem("out_stored")
        w_hi_done = sem("w_hi_done")
        w_split = sem("w_split")
        chunk_done = sem("chunk_done")
        x_hi_done = sem("x_hi_done")
        x_split = sem("x_split")
        squared = sem("squared")
        ss_added = sem("ss_added")
        pool_const = sem("pool_const")
        pool_woken = sem("pool_woken")
        vec_const = sem("vec_const")
        eye_ready = sem("eye_ready")
        ms_summed = sem("ms_summed")
        ms_ready = sem("ms_ready")
        rstd_ready = sem("rstd_ready")
        diag_ready = sem("diag_ready")
        rstd_spread = sem("rstd_spread")
        qk_scaled = sem("qk_scaled")
        qk_hi_done = sem("qk_hi_done")
        qk_ready = sem("qk_ready")
        scores_done = sem("scores_done")
        z_abs = sem("z_abs")
        z_exp = sem("z_exp")
        z_ln = sem("z_ln")
        softplus_done = sem("softplus_done")
        softplus_masked = sem("softplus_masked")
        softplus_hi = sem("softplus_hi")
        softplus_ready = sem("softplus_ready")
        v_hi_done = sem("v_hi_done")
        v_ready = sem("v_ready")
        wp_hi_done = sem("wp_hi_done")
        wp_ready = sem("wp_ready")
        logits_done = sem("logits_done")
        weights_exp = sem("weights_exp")
        weights_masked = sem("weights_masked")
        weights_hi = sem("weights_hi")
        weights_ready = sem("weights_ready")
        y_done = sem("y_done")
        y_free = sem("y_free")
        gate_drained = sem("gate_drained")
        gate_abs = sem("gate_abs")
        gate_exp = sem("gate_exp")
        gate_ln = sem("gate_ln")
        gate_logsig = sem("gate_logsig")
        gate_sig = sem("gate_sig")
        gate_done = sem("gate_done")
        u_drained = sem("u_drained")
        u_summed = sem("u_summed")
        u_window = sem("u_window")
        u_fixed = sem("u_fixed")
        u_mixed = sem("u_mixed")
        mixed_hi_done = sem("mixed_hi_done")
        mixed_ready = sem("mixed_ready")
        pool_done = sem("pool_done")
        pool_free = sem("pool_free")
        mix_hi_done = sem("mix_hi_done")
        mix_split = sem("mix_split")
        rows_done = sem("rows_done")
        rows_free = sem("rows_free")
        rows_squared = sem("rows_squared")
        out_summed = sem("out_summed")
        out_ms_ready = sem("out_ms_ready")
        out_rstd_ready = sem("out_rstd_ready")
        final_done = sem("final_done")

        POOL_CONSTS = 4
        LAST_SLOTS = (2, 3, 0, 1)
        H0 = V_CHUNKS
        O0 = V_CHUNKS + HEAD_CHUNKS
        N_CHUNKS = O0 + OUT_CHUNKS

        def raw_loads(n, slot):
            return n // 2 + slot

        FINAL_PIECES = 2

        def final_pieces(s):
            n = FINAL_PIECES if s < TT - 1 else 2 * FINAL_PIECES
            return [(i * D // n, (i + 1) * D // n) for i in range(n)]

        def act_tile(t, k):
            return t[:, k * SEQ:(k + 1) * SEQ]

        block = ctx.enter_context(nc.Block())

        @block.sync
        def _(sp):
            def load_x(i):
                a, b = X_PIECES[i]
                sp.dma_start(mix[:, a * SEQ:b * SEQ], xT[:, a * SEQ:b * SEQ]).then_inc(x_loaded[i], 16)

            for i, (a, b) in enumerate(W0_PIECES):
                load_x(i)
                sp.dma_start(w_raw[0][:, a * BANK:b * BANK],
                             w_v[0][:, a * BANK:b * BANK]).then_inc(w0_loaded[i], 16)
                if i == 0:
                    sp.dma_start(pre_gain_col[:, :], pre_gain).then_inc(gain_loaded, 16)
            load_x(3)
            for n in range(1, V_CHUNKS):
                if n == 2:
                    load_x(4)
                    load_x(5)
                if n >= 2:
                    sp.wait_ge(w_split, n - 1)
                sp.dma_start(w_raw[n % 2][:, :], w_v[n]).then_inc(raw_loaded[n % 2], 16)
                if n == 1:
                    sp.dma_start(pool_scale_col[:, :], pool_scale).then_inc(scale_loaded, 16)
                if n == 3:
                    sp.dma_start(post_gain_rows[:, :],
                                 post_gain.partition_broadcast(P)).then_inc(rows_gain_loaded, 16)
            with sp.Fori(0, HEADS // 2) as i:
                for j in range(2):
                    for m in range(PER_HEAD):
                        at = PER_HEAD * j + m
                        n = H0 + 2 * PER_HEAD * i + at
                        sp.wait_ge(w_split, n - 1)
                        sp.dma_start(w_raw[at % 2][:, :],
                                     w_heads[2 * PER_HEAD * i + at]).then_inc(raw_loaded[at % 2], 16)
                        if m == 1:
                            sp.wait_ge(wp_ready, 2 * i + j + 1)
                            sp.dma_start(wp_raw[:, :], w_pool[2 * i + j]).then_inc(wp_loaded, 16)
            with sp.Fori(0, OUT_CHUNKS // 4) as dc:
                for kk in range(4):
                    sp.wait_ge(w_split, O0 + 4 * dc + kk - 1)
                    sp.dma_start(w_raw[kk % 2][:, :], w_out[4 * dc + kk]).then_inc(raw_loaded[kk % 2], 16)
            for s in range(2):
                sp.wait_ge(w_split, N_CHUNKS - 1 + s)
                sp.dma_start(w_raw[s][:, :], x[s]).then_inc(raw_loaded[s], 16)
            for s in range(TT):
                for i, (a, b) in enumerate(final_pieces(s)):
                    sp.wait_ge(final_done, FINAL_PIECES * s + i + 1)
                    sp.dma_start(out[s][:, a:b], mix[:, s * D + a:s * D + b]).then_inc(out_stored, 16)
                if s + 2 < TT:
                    sp.dma_start(w_raw[s % 2][:, :], x[s + 2]).then_inc(raw_loaded[s % 2], 16)
            sp.wait_ge(out_stored, 16 * sum(len(final_pieces(s)) for s in range(TT)))

        @block.scalar
        def _(act):
            act.preload_act_table_set("natural_log_exp_and_others")

            def w_hi_of(n, raw, slot, count):
                act.wait_ge(raw_loaded[raw], 16 * count)
                act.activation(w_hi[slot][:, :], w_raw[raw][:, :], ACT.Copy).then_inc(w_hi_done, 1)

            def x_hi_of(piece):
                act.wait_ge(x_loaded[piece], 16)
                for k in range(*X_PIECES[piece]):
                    act.activation(act_tile(act_hi, k), act_tile(mix, k), ACT.Copy,
                                   scale=pre_gain_col[:, k:k + 1]).then_inc(x_hi_done, 1)

            def square_of(k):
                if k >= 3:
                    act.wait_ge(ss_added, k - 2)
                dst = ss_part[:, :] if k == 0 else square[k % 2]
                act.activation(dst, act_tile(mix, k), ACT.Square).then_inc(squared, 1)

            act.wait_ge(gain_loaded, 16)
            for i, (a, b) in enumerate(W0_PIECES):
                x_hi_of(i)
                act.wait_ge(w0_loaded[i], 16)
                act.activation(w_hi[0][:, a * BANK:b * BANK], w_raw[0][:, a * BANK:b * BANK],
                               ACT.Copy).then_inc(w0_hi_done if b < KC else w_hi_done, 1)
            x_hi_of(3)
            w_hi_of(1, 1, 1, raw_loads(1, 1))
            x_hi_of(4)
            x_hi_of(5)
            for n in range(V_CHUNKS):
                act.wait_ge(chunk_done, n + 1)
                w_hi_of(n + 2, n % 2, n % 2, raw_loads(n + 2, n % 2))
                if n < 2:
                    for k in range(n * KT // 2, (n + 1) * KT // 2):
                        square_of(k)

            def gate(h, which):
                n = 2 * h + which + 1
                act.wait_ge(gate_drained, n + 1)
                act.activation(work[:, :], drained[:, :], ACT.Abs).then_inc(gate_abs, 1)
                act.wait_ge(gate_abs, n)
                act.activation(work[:, :], work[:, :], ACT.Exp, scale=-1.0).then_inc(gate_exp, 1)
                act.wait_ge(gate_exp, n)
                act.activation(work[:, :], work[:, :], ACT.Ln, bias=1.0).then_inc(gate_ln, 1)
                act.wait_ge(gate_logsig, n)
                act.activation(work[:, :], work[:, :], ACT.Exp).then_inc(gate_sig, 1)

            def mix_hi(*tiles):
                for k in tiles:
                    act.activation(act_tile(act_hi, k), act_tile(mix, k),
                                   ACT.Copy).then_inc(mix_hi_done, 1)

            def head_pair(i, last=False):
                for j in range(2):
                    h = 2 * i + j
                    for m in range(PER_HEAD):
                        at = PER_HEAD * j + m
                        n = H0 + 2 * PER_HEAD * i + at
                        act.wait_ge(chunk_done, n + 1)
                        if last and at == 2 * PER_HEAD - 1:
                            mix_hi(*range(KC))
                        w_hi_of(n + 2, at % 2, at % 2, PER_HEAD * i + raw_loads(H0 + at + 2, at % 2))
                        if m == 1:
                            act.wait_ge(scores_done, h + 1)
                            act.activation(tri[:, :], scores, ACT.Abs).then_inc(z_abs, 1)
                            act.wait_ge(z_abs, h + 1)
                            act.activation(tri[:, :], tri[:, :], ACT.Exp, scale=-1.0).then_inc(z_exp, 1)
                            act.wait_ge(z_exp, h + 1)
                            act.activation(tri[:, :], tri[:, :], ACT.Ln, bias=1.0).then_inc(z_ln, 1)
                        if m == 2:
                            act.wait_ge(softplus_masked, 2 * h + 2)
                            act.activation(tri_hi[:, :], tri[:, :], ACT.Copy).then_inc(softplus_hi, 1)
                            gate(h, 0)
                        if m == 3:
                            act.wait_ge(logits_done, h + 1)
                            act.activation(tri[:, :], scores, ACT.Exp).then_inc(weights_exp, 1)
                            act.wait_ge(weights_masked, 2 * h + 2)
                            act.activation(tri_hi[:, :], tri[:, :], ACT.Copy).then_inc(weights_hi, 1)
                        if m == 4:
                            gate(h, 1)

            with act.Fori(0, HEADS // 2 - 1) as i:
                head_pair(i)
            head_pair(HEADS // 2 - 1, last=True)
            mix_hi(*range(KC, HEADS - 1))
            act.wait_ge(y_free, 1 + HEADS)
            mix_hi(*range(HEADS - 1, KT - 2))
            act.wait_ge(pool_free, 1 + 2 * GROUPS)
            mix_hi(KT - 2, KT - 1)

            def rows_square(s, dc):
                act.activation(bank(ACC + s), bank(ROWS + s), ACT.Square,
                               accum_out=out_ss[:, bass.ds(4 * s + dc, 1)]).then_inc(rows_squared, 1)

            def rows_round(dc, last):
                for kk in range(KK):
                    n = O0 + KK * dc + kk
                    if last and kk == 2:
                        for m in range(2):
                            w_hi_of(n + 2 + m, m, LAST_SLOTS[m], raw_loads(N_CHUNKS - KK + m, m))
                    if kk == 3:
                        for s in range(TT - 1):
                            act.wait_ge(rows_done, 3 * (2 + dc) + s + 1)
                            rows_square(s, dc)
                    act.wait_ge(chunk_done, n + 1)
                    if last and kk >= 2:
                        w_hi_of(n + 4, kk % 2, LAST_SLOTS[kk], raw_loads(N_CHUNKS - KK + kk, kk % 2))
                    else:
                        w_hi_of(n + 2, kk % 2, kk % 2, 2 * dc + raw_loads(O0 + kk + 2, kk % 2))
                rows_square(TT - 1, dc)

            with act.Fori(0, 2) as dc:
                rows_round(dc, False)
            rows_round(2, True)
            for s in range(TT):
                act.wait_ge(rows_done, 3 * 5 + s + 1)
                rows_square(s, 3)

        @block.vector
        def _(dve):
            for free in (u_drained, gate_drained, gate_done, y_free, pool_free, wp_ready):
                dve.sem_inc(free, 1)
            dve.memset(neg_half[:, :], -0.5).then_inc(vec_const, 1)
            dve.memset(ones_col[:, :], 1.0).then_inc(vec_const, 1)
            dve.memset(ones_sq, 1.0).then_inc(vec_const, 1)
            for g, w in enumerate(WINDOWS):
                dve.memset(inv_window[:, g:g + 1], 1.0 / w).then_inc(vec_const, 1)
            VEC = 3 + GROUPS

            def w_lo_of(n, raw, slot):
                dve.wait_ge(w_hi_done, n + 1)
                dve.tensor_tensor(w_lo[slot][:, :], w_raw[raw][:, :], w_hi[slot][:, :].bitcast(F32),
                                  ALU.subtract).then_inc(w_split, 1)

            def x_lo_of(piece):
                for k in range(*X_PIECES[piece]):
                    dve.wait_ge(x_hi_done, k + 1)
                    dve.scalar_tensor_tensor(act_tile(act_lo, k), act_tile(mix, k),
                                             pre_gain_col[:, k:k + 1],
                                             act_tile(act_hi, k).bitcast(F32),
                                             ALU.mult, ALU.subtract).then_inc(x_split, 1)

            def add_square(k):
                dve.wait_ge(squared, k + 1)
                if k >= 2:
                    dve.wait_ge(ss_added, k - 1)
                dve.tensor_tensor(ss_part[:, :], ss_part[:, :], square[k % 2],
                                  ALU.add).then_inc(ss_added, 1)

            dve.wait_ge(gain_loaded, 16)
            for i, (a, b) in enumerate(W0_PIECES):
                x_lo_of(i)
                dve.wait_ge(*((w0_hi_done, i + 1) if b < KC else (w_hi_done, 1)))
                dve.tensor_tensor(w_lo[0][:, a * BANK:b * BANK], w_raw[0][:, a * BANK:b * BANK],
                                  w_hi[0][:, a * BANK:b * BANK].bitcast(F32),
                                  ALU.subtract).then_inc(w0_split if b < KC else w_split, 1)
            x_lo_of(3)
            w_lo_of(1, 1, 1)
            x_lo_of(4)
            x_lo_of(5)
            dve.wait_ge(pool_const, 1)
            dve.reciprocal(positions[:, :], positions[:, :]).then_inc(vec_const, 1)
            dve.wait_ge(vec_const, VEC + 1)
            for g, w in enumerate(WINDOWS):
                dve.tensor_scalar(count_fix[:, g * MAX_WINDOW:(g + 1) * MAX_WINDOW], positions[:, :],
                                  float(w), 1.0, ALU.mult, ALU.max).then_inc(vec_const, 1)

            def v_rows_of(g, s):
                if s < TT - 1:
                    dve.wait_ge(rows_done, 3 * g + s + 1)
                else:
                    dve.wait_ge(chunk_done, KK * (g + 1))
                ins = dve.tensor_scalar(v_rows[:, s * D_SB + g * BANK:s * D_SB + (g + 1) * BANK],
                                        bank(ROWS + s), rstd_col[:, s:s + 1], None, ALU.mult)
                ins.then_inc(rows_free, 1)

            for n in range(V_CHUNKS):
                w_lo_of(n + 2, n % 2, n % 2)
                if n < 2:
                    for k in range(max(1, n * KT // 2), (n + 1) * KT // 2):
                        add_square(k)
                if n == 2:
                    dve.wait_ge(ms_summed, 1)
                    dve.tensor_scalar(ms_col[:, :], ms_ps, 1.0 / D, EPS, ALU.mult,
                                      ALU.add).then_inc(ms_ready, 1)
                    dve.wait_ge(rstd_ready, 1)
                    dve.wait_ge(eye_ready, 2)
                    for s in range(TT):
                        dve.tensor_scalar(rstd_diag[:, s * P:(s + 1) * P], eye, rstd_col[:, s:s + 1],
                                          None, ALU.mult).then_inc(diag_ready, 1)
                    for s in range(TT):
                        v_rows_of(0, s)
                if n == 3:
                    dve.wait_ge(rstd_spread, 1)
                    dve.tensor_copy(rstd_rows[:, :], rstd_ps).then_inc(rstd_ready, 1)
                    dve.memset(cumsum[:, 0:MAX_WINDOW], 0.0).then_inc(vec_const, 1)
                if n == V_CHUNKS - 2:
                    for s in range(TT):
                        v_rows_of(1, s)
            dve.wait_ge(scale_loaded, 16)
            dve.wait_ge(rstd_ready, 2)
            dve.wait_ge(rows_free, 2 * TT)
            dve.wait_ge(vec_const, VEC + 2 + GROUPS)

            def drain_qk(at, n, count, hi, lo, scale):
                dve.wait_ge(chunk_done, n + 1)
                if hi is q_hi:
                    dve.wait_ge(gate_done, count)
                else:
                    dve.wait_ge(qk_ready, count - 1)
                dve.scalar_tensor_tensor(drained[:, :], bank(ACC + at % 2), scale, rstd_rows[:, :],
                                         ALU.mult, ALU.mult).then_inc(qk_scaled, 1)
                dve.wait_ge(qk_scaled, count)
                dve.tensor_copy(hi[:, :], drained[:, :]).then_inc(qk_hi_done, 1)
                dve.wait_ge(qk_hi_done, count)
                dve.tensor_tensor(lo[:, :], drained[:, :], hi[:, :].bitcast(F32),
                                  ALU.subtract).then_inc(qk_ready, 1)

            def drain_gate(at, n):
                dve.wait_ge(chunk_done, n + 1)
                dve.tensor_tensor(drained[:, :], bank(ACC + at % 2), rstd_rows[:, :],
                                  ALU.mult).then_inc(gate_drained, 1)

            def gate(h, which, tile):
                n = 2 * h + which + 1
                dve.wait_ge(gate_ln, n)
                dve.scalar_tensor_tensor(work[:, :], drained[:, :], 0.0, work[:, :],
                                         ALU.min, ALU.subtract).then_inc(gate_logsig, 1)
                dve.wait_ge(gate_sig, n)
                dve.tensor_tensor(mix[:, bass.ds(tile * SEQ, SEQ)], drained[:, :], work[:, :],
                                  ALU.mult).then_inc(gate_done, 1)

            def mix_lo(*tiles):
                for k in tiles:
                    dve.wait_ge(mix_hi_done, k + 1)
                    dve.tensor_tensor(act_tile(act_lo, k), act_tile(mix, k),
                                      act_tile(act_hi, k).bitcast(F32),
                                      ALU.subtract).then_inc(mix_split, 1)

            def head_pair(i, lagged, last=False):
                for j in range(2):
                    h = 2 * i + j
                    at = PER_HEAD * j
                    n = H0 + 2 * PER_HEAD * i + at
                    drain_qk(at, n, 2 * h + 1, q_hi, q_lo, SCALE)
                    w_lo_of(n + 2, at % 2, at % 2)
                    at, n = at + 1, n + 1
                    drain_qk(at, n, 2 * h + 2, k_hi, k_lo, 1.0)
                    w_lo_of(n + 2, at % 2, at % 2)
                    dve.wait_ge(z_ln, h + 1)
                    dve.scalar_tensor_tensor(tri[:, :], scores, 0.0, tri[:, :],
                                             ALU.max, ALU.add).then_inc(softplus_done, 1)
                    at, n = at + 1, n + 1
                    drain_gate(at, n)
                    w_lo_of(n + 2, at % 2, at % 2)
                    dve.wait_ge(softplus_hi, h + 1)
                    dve.tensor_tensor(tri_lo[:, :], tri[:, :], tri_hi[:, :].bitcast(F32),
                                      ALU.subtract).then_inc(softplus_ready, 1)
                    dve.wait_ge(v_hi_done, h + 1)
                    dve.tensor_tensor(q_lo[:, :].rearrange("p (b d) -> p b d", b=TT),
                                      v_rows[:, :].rearrange("p (b c) -> p b c", b=TT)
                                      [:, :, bass.ds(h * HD, HD)],
                                      q_hi[:, :].rearrange("p (b d) -> p b d", b=TT).bitcast(F32),
                                      ALU.subtract).then_inc(v_ready, 1)
                    dve.wait_ge(wp_hi_done, h + 1)
                    dve.tensor_tensor(k_lo[:, 0:2 * P], wp_raw[:, :], k_hi[:, 0:2 * P].bitcast(F32),
                                      ALU.subtract).then_inc(wp_ready, 1)
                    gate(h, 0, h)
                    at, n = at + 1, n + 1
                    dve.wait_ge(chunk_done, n + 1)
                    dve.wait_ge(gate_done, 2 * h + 2)
                    dve.tensor_tensor(drained[:, :], bank(ACC + at % 2), rstd_rows[:, :],
                                      ALU.mult).then_inc(u_drained, 1)
                    dve.wait_ge(u_drained, h + 2)
                    dve.tensor_tensor_scan(cumsum[:, MAX_WINDOW:], ones_col[:, 0:1].to_broadcast([P, SEQ]),
                                           drained[:, :], 0.0, ALU.mult, ALU.add).then_inc(u_summed, 1)
                    w_lo_of(n + 2, at % 2, at % 2)
                    dve.wait_ge(u_summed, h + 1)
                    dve.tensor_tensor(work[:, :], cumsum[:, MAX_WINDOW:],
                                      cumsum[:, bass.ds(lagged, SEQ)],
                                      ALU.subtract).then_inc(u_window, 1)
                    dve.wait_ge(u_window, h + 1)
                    dve.tensor_tensor(work[:, 0:MAX_WINDOW], work[:, 0:MAX_WINDOW],
                                      count_fix[:, bass.ds(i * MAX_WINDOW, MAX_WINDOW)],
                                      ALU.mult).then_inc(u_fixed, 1)
                    dve.wait_ge(u_fixed, h + 1)
                    dve.scalar_tensor_tensor(work[:, :], work[:, :], inv_window[:, bass.ds(i, 1)],
                                             drained[:, :], ALU.mult, ALU.subtract).then_inc(u_mixed, 1)
                    dve.wait_ge(u_mixed, h + 1)
                    dve.tensor_copy(mixed_hi[:, :], work[:, :]).then_inc(mixed_hi_done, 1)
                    dve.wait_ge(mixed_hi_done, h + 1)
                    dve.tensor_tensor(mixed_lo[:, :], work[:, :], mixed_hi[:, :].bitcast(F32),
                                      ALU.subtract).then_inc(mixed_ready, 1)
                    dve.wait_ge(weights_hi, h + 1)
                    dve.tensor_tensor(tri_lo[:, :], tri[:, :], tri_hi[:, :].bitcast(F32),
                                      ALU.subtract).then_inc(weights_ready, 1)
                    at, n = at + 1, n + 1
                    dve.wait_ge(mixed_ready, h + 1)
                    drain_gate(at, n)
                    if last and j == 1:
                        mix_lo(*range(KC))
                    w_lo_of(n + 2, at % 2, at % 2)
                    dve.wait_ge(y_done, h + 1)
                    dve.tensor_tensor(mix[:, bass.ds(h * SEQ, SEQ)], bank(Y),
                                      mix[:, bass.ds(h * SEQ, SEQ)], ALU.mult).then_inc(y_free, 1)
                    gate(h, 1, HEADS + h)
                    if j == 1:
                        dve.wait_ge(pool_done, i + 1)
                        dve.wait_ge(gate_done, 2 * h + 3)
                        for t in range(2):
                            rows = mix[:, bass.ds((HEADS + 2 * i + t) * SEQ, SEQ)]
                            dve.scalar_tensor_tensor(rows, bank(POOL + t),
                                                     pool_scale_col[:, bass.ds(2 * i + t, 1)], rows,
                                                     ALU.mult, ALU.mult).then_inc(pool_free, 1)

            with dve.Fori(0, HEADS // 2 - 1) as i:
                head_pair(i, dve.snap(dve.to_reg(MAX_WINDOW - (2 << i)), min_val=0,
                                      max_val=MAX_WINDOW - 2))
            head_pair(HEADS // 2 - 1, MAX_WINDOW - WINDOWS[-1], last=True)
            mix_lo(*range(KC, KT))

            def rows_gain(s, dc):
                dve.tensor_tensor(mix[:, bass.ds(s * D + dc * BANK, BANK)], bank(ROWS + s),
                                  post_gain_rows[:, bass.ds(dc * BANK, BANK)],
                                  ALU.mult).then_inc(rows_free, 1)

            dve.wait_ge(rows_gain_loaded, 16)
            dve.wait_ge(mix_split, KT)
            def rows_round(dc, last):
                for kk in range(KK):
                    n = O0 + KK * dc + kk
                    if last and kk == 2:
                        for m in range(2):
                            w_lo_of(n + 2 + m, m, LAST_SLOTS[m])
                    if kk == 3:
                        for s in range(TT - 1):
                            dve.wait_ge(rows_squared, 4 * dc + s + 1)
                            rows_gain(s, dc)
                    if last and kk >= 2:
                        w_lo_of(n + 4, kk % 2, LAST_SLOTS[kk])
                    else:
                        w_lo_of(n + 2, kk % 2, kk % 2)
                dve.wait_ge(rows_squared, 4 * dc + TT)
                rows_gain(TT - 1, dc)

            with dve.Fori(0, 2) as dc:
                rows_round(dc, False)
            rows_round(2, True)
            for s in range(TT):
                dve.wait_ge(rows_squared, 12)
                dve.tensor_reduce(out_ms[:, s:s + 1], out_ss[:, 4 * s:4 * s + 3], AX_X,
                                  ALU.add).then_inc(out_summed, 1)
                dve.wait_ge(out_summed, 2 * s + 1)
                dve.tensor_scalar(out_ms[:, s:s + 1], out_ms[:, s:s + 1], D * EPS, None,
                                  ALU.add).then_inc(out_summed, 1)
                dve.wait_ge(out_summed, 2 * s + 2)
                dve.wait_ge(rows_squared, 12 + s + 1)
                dve.tensor_scalar(out_ms[:, s:s + 1], out_ss[:, 4 * s + 3:4 * s + 4],
                                  out_ms[:, s:s + 1], 1.0 / D, ALU.add,
                                  ALU.mult).then_inc(out_ms_ready, 1)
                rows_gain(s, 3)
                dve.wait_ge(out_rstd_ready, s + 1)
                dve.wait_ge(raw_loaded[s % 2], 16 * raw_loads(N_CHUNKS + s, s % 2))
                dve.wait_ge(rows_free, 2 * TT + 12 + s + 1)
                for a, b in final_pieces(s):
                    rows = mix[:, s * D + a:s * D + b]
                    dve.scalar_tensor_tensor(rows, rows, out_rstd[:, s:s + 1], w_raw[s % 2][:, a:b],
                                             ALU.mult, ALU.add).then_inc(final_done, 1)

        @block.gpsimd
        def _(pool):
            pool.iota(positions[:, :], [[1, MAX_WINDOW]], base=1, channel_multiplier=0,
                      allow_small_or_imprecise_dtypes=True).then_inc(pool_const, 1)
            pool.memset(eye, 0.0).then_inc(eye_ready, 1)
            pool.wait_ge(eye_ready, 1)
            pool.affine_select(out=eye, in_=eye, compare_op=ALU.not_equal, fill=1.0, base=0,
                               pattern=[[-1, P]], channel_multiplier=1).then_inc(eye_ready, 1)
            pool.memset(fill, -1.0).then_inc(pool_const, 1)
            pool.wait_ge(pool_const, 2)
            pool.tensor_copy(neg_ones[:, :], fill).then_inc(pool_const, 1)
            pool.affine_select(out=neg_tri[:, :], in_=fill, compare_op=ALU.is_ge, fill=0.0, base=0,
                               pattern=[[-1, P]], channel_multiplier=1).then_inc(pool_const, 1)
            pool.wait_ge(ms_ready, 1)
            pool.wait_ge(vec_const, 1)
            pool.tensor_tensor(rstd_col[:, :], ms_col[:, :], neg_half[:, 0:1].to_broadcast([P, TT]),
                               ALU.pow).then_inc(rstd_ready, 1)

            def mask(done):
                for first, step in ((START[0], START[1] - START[0]), (START[3], START[2] - START[3])):
                    sq = tri[:, first:first + 2 * step].rearrange("p (b c) -> p b c", b=2)[:, :, 0:P]
                    pool.affine_select(out=sq, in_=sq, compare_op=ALU.is_gt, fill=0.0, base=0,
                                       pattern=[[0, 2], [1, P]], channel_multiplier=-1).then_inc(done, 1)

            with pool.Fori(0, HEADS // 2) as i:
                for j in range(2):
                    h = 2 * i + j
                    pool.wait_ge(scores_done, h + 1)
                    pool.tensor_copy(q_hi[:, :].rearrange("p (b d) -> p b d", b=TT),
                                     v_rows[:, :].rearrange("p (b c) -> p b c", b=TT)
                                     [:, :, bass.ds(h * HD, HD)]).then_inc(v_hi_done, 1)
                    pool.wait_ge(wp_loaded, 16 * (h + 1)).then_inc(pool_woken, 1)
                    pool.tensor_copy(k_hi[:, 0:2 * P], wp_raw[:, :]).then_inc(wp_hi_done, 1)
                    pool.wait_ge(softplus_done, h + 1).then_inc(pool_woken, 1)
                    mask(softplus_masked)
                    pool.wait_ge(weights_exp, h + 1).then_inc(pool_woken, 1)
                    mask(weights_masked)

            for s in range(TT):
                pool.wait_ge(out_ms_ready, s + 1)
                pool.tensor_tensor(out_rstd[:, s:s + 1], out_ms[:, s:s + 1], neg_half[:, 0:1],
                                   ALU.pow).then_inc(out_rstd_ready, 1)

        @block.tensor
        def _(pe):
            def three(dst, sta, mov, first, last):
                pe.matmul(dst, sta[0], mov[0], start=first, stop=False, skip_group_check=True)
                pe.matmul(dst, sta[0], mov[1], start=False, stop=False, skip_group_check=True)
                return pe.matmul(dst, sta[1], mov[0], start=False, stop=last, skip_group_check=True)

            def both(pair, a, b):
                return pair[0][:, a:b], pair[1][:, a:b]

            acts = (act_hi, act_lo)
            ws = list(zip(w_hi, w_lo))

            def rows_tile(s, kk, slot):
                for k in range(KC):
                    a = (kk * KC + k) * SEQ + s * P
                    mm = three(bank(ROWS + s), both(acts, a, a + P),
                               both(ws[slot], k * BANK, (k + 1) * BANK),
                               kk == 0 and k == 0, kk == KK - 1 and k == KC - 1)
                return mm

            for g in range(2):
                for kk in range(KK):
                    n = KK * g + kk
                    if n < 2:
                        for k in range(KC):
                            if n == 0 and k == 0:
                                pe.wait_ge(w0_hi_done, 1)
                                pe.wait_ge(x_hi_done, 1)
                                for s in range(TT):
                                    pe.matmul(bank(ROWS + s), act_hi[:, s * P:(s + 1) * P],
                                              w_hi[0][:, 0:BANK], start=True, stop=False,
                                              skip_group_check=True)
                                pe.wait_ge(x_split, 1)
                                pe.wait_ge(w0_split, 1)
                                for s in range(TT):
                                    pe.matmul(bank(ROWS + s), act_hi[:, s * P:(s + 1) * P],
                                              w_lo[0][:, 0:BANK], start=False, stop=False,
                                              skip_group_check=True)
                                    pe.matmul(bank(ROWS + s), act_lo[:, s * P:(s + 1) * P],
                                              w_hi[0][:, 0:BANK], start=False, stop=False,
                                              skip_group_check=True)
                                continue
                            if n == 0 and k < KC // 2:
                                pe.wait_ge(w0_split, k + 1)
                            else:
                                pe.wait_ge(w_split, n + 1)
                            pe.wait_ge(x_split, n * KC + k + 1)
                            for s in range(TT):
                                a = (n * KC + k) * SEQ + s * P
                                mm = three(bank(ROWS + s), both(acts, a, a + P),
                                           both(ws[n], k * BANK, (k + 1) * BANK), False, False)
                    else:
                        pe.wait_ge(w_split, n + 1)
                        pe.wait_ge(x_split, min(KT, KC * (n + 1)))
                        for s in range(TT):
                            if kk == 0 and g == 1:
                                pe.wait_ge(rows_free, s + 1)
                            mm = rows_tile(s, kk, n % 2)
                            if kk == KK - 1 and s < TT - 1:
                                mm.then_inc(rows_done, 1)
                            if n == 3 and s == 1:
                                pe.wait_ge(ss_added, KT - 1)
                                pe.wait_ge(vec_const, 3)
                                for t in range(TT):
                                    ms = pe.matmul(ms_ps[:, t:t + 1], ss_part[:, t * P:(t + 1) * P],
                                                   ones_col[:, 0:1], start=True, stop=True)
                                ms.then_inc(ms_summed, 1)
                    mm.then_inc(chunk_done, 1)
                    if n == 3:
                        pe.wait_ge(diag_ready, TT)
                        pe.matmul(rstd_ps, ones_sq, rstd_diag, start=True,
                                  stop=True).then_inc(rstd_spread, 1)

            def column_tiles(at, k0, k1):
                for k in range(k0, k1):
                    mm = three(bank(ACC + at % 2), both(ws[at % 2], k * P, (k + 1) * P),
                               both(acts, k * SEQ, (k + 1) * SEQ), k == 0, k == KT - 1)
                return mm

            def tri_part(b, skip=0):
                return START[b] + skip * P, START[b] + WIDTH[b]

            def qk(h):
                pe.wait_ge(qk_ready, 2 * h + 2)
                for b in range(TT):
                    a, z = tri_part(b)
                    mm = three(ps[:, a:z], both((k_hi, k_lo), b * P, (b + 1) * P),
                               both((q_hi, q_lo), b * P, SEQ), b < 3, False)
                mm.then_inc(scores_done, 1)

            def suffix_sums(h):
                pe.wait_ge(softplus_ready, h + 1)
                for b in range(TT):
                    for later in range(b, TT):
                        a, z = tri_part(b, later - b)
                        src, end = tri_part(later)
                        sta = neg_tri if later == b else neg_ones
                        pe.matmul(ps[:, a:z], sta[:, :], tri_hi[:, src:end], start=False,
                                  stop=False, skip_group_check=True)
                        mm = pe.matmul(ps[:, a:z], sta[:, :], tri_lo[:, src:end], start=False,
                                       stop=later == TT - 1, skip_group_check=True)
                mm.then_inc(logits_done, 1)

            def weighted_values(h):
                pe.wait_ge(weights_ready, h + 1)
                pe.wait_ge(v_ready, h + 1)
                pe.wait_ge(y_free, h + 1)
                for b in range(TT):
                    a, z = tri_part(b)
                    mm = three(bank(Y)[:, b * P:], both((q_hi, q_lo), b * P, (b + 1) * P),
                               both((tri_hi, tri_lo), a, z), b == 0, b == TT - 1)
                mm.then_inc(y_done, 1)

            def pool_tiles(i, j):
                pe.wait_ge(mixed_ready, 2 * i + j + 1)
                pe.wait_ge(wp_ready, 2 * i + j + 2)
                if j == 0:
                    pe.wait_ge(pool_free, 2 * i + 1)
                for t in range(2):
                    mm = three(bank(POOL + t), both((k_hi, k_lo), t * P, (t + 1) * P),
                               both((mixed_hi, mixed_lo), 0, SEQ), j == 0, j == 1)
                if j == 1:
                    mm.then_inc(pool_done, 1)

            pe.wait_ge(pool_const, POOL_CONSTS)
            with pe.Fori(0, HEADS // 2) as i:
                for j in range(2):
                    h = 2 * i + j
                    for m in range(PER_HEAD):
                        at = PER_HEAD * j + m
                        n = H0 + 2 * PER_HEAD * i + at
                        pe.wait_ge(w_split, n + 1)
                        if m == 0:
                            pe.wait_ge(u_drained, h + 1)
                        if m == 1:
                            pe.wait_ge(gate_drained, 2 * h + 1)
                        if m == 2:
                            pe.wait_ge(qk_scaled, 2 * h + 1)
                        if m == 3:
                            pe.wait_ge(qk_scaled, 2 * h + 2)
                        if m == 4:
                            pe.wait_ge(gate_drained, 2 * h + 2)
                        if m == 2:
                            column_tiles(at, 0, KT // 2)
                            qk(h)
                            column_tiles(at, KT // 2, KT).then_inc(chunk_done, 1)
                        else:
                            column_tiles(at, 0, KT).then_inc(chunk_done, 1)
                        if m == 3:
                            suffix_sums(h)
                    weighted_values(h)
                    pool_tiles(i, j)

            with pe.Fori(0, 3) as dc:
                for kk in range(KK):
                    n = O0 + KK * dc + kk
                    pe.wait_ge(w_split, n + 1)
                    pe.wait_ge(mix_split, KC * (kk + 1))
                    for s in range(TT):
                        if kk == 0:
                            pe.wait_ge(rows_free, 4 * dc + s + 5)
                            if s == Y:
                                pe.wait_ge(y_free, 1 + HEADS)
                        mm = rows_tile(s, kk, kk % 2)
                        if kk == KK - 1 and s < TT - 1:
                            mm.then_inc(rows_done, 1)
                    mm.then_inc(chunk_done, 1)
            for s in range(TT):
                pe.wait_ge(rows_free, 4 * 3 + s + 5)
                for kk in range(KK):
                    if s == 0:
                        pe.wait_ge(w_split, N_CHUNKS - KK + kk + 1)
                    mm = rows_tile(s, kk, LAST_SLOTS[kk])
                mm.then_inc(rows_done, 1)


def kernel(x, pre_norm_gain, w_in, w_pool, pool_scale, w_out, post_norm_gain):
    import numpy as np
    import concourse.bacc as bacc
    from concourse.bass_utils import run_bass_kernel_spmd

    x, w_in, w_out = np.asarray(x)[0], np.asarray(w_in)[0], np.asarray(w_out)[0]
    w_pool = np.asarray(w_pool)[0]

    def features_first(a):
        return a.reshape(-1, P, a.shape[-1]).transpose(1, 0, 2)

    def moving(w):
        c = w.reshape(KT // KC, KC, P, -1, BANK).transpose(3, 0, 2, 1, 4)
        return c.reshape(-1, P, CHUNK)

    parts = w_in.reshape(KT, P, 6, HEADS, P).transpose(3, 2, 1, 0, 4)
    heads = parts[:, [0, 1, 3, 4, 5]].reshape(HEAD_CHUNKS, P, CHUNK)
    arrays = {
        "xT": features_first(x.T).reshape(P, KT * SEQ),
        "x": x.reshape(TT, P, D),
        "pre_gain": np.asarray(pre_norm_gain).reshape(KT, P).T,
        "w_v": moving(w_in[:, 2 * D_SB:3 * D_SB]),
        "w_heads": heads,
        "w_pool": w_pool.reshape(2 * GROUPS, P, 2 * P),
        "pool_scale": np.asarray(pool_scale).reshape(2 * GROUPS, P).T,
        "w_out": moving(w_out),
        "post_gain": np.asarray(post_norm_gain).reshape(D),
    }
    arrays = {name: np.ascontiguousarray(a) for name, a in arrays.items()}
    nc = bacc.Bacc("TRN2", target_bir_lowering=False, num_devices=1)
    args = {name: nc.dram_tensor(name, a.shape, F32, kind="ExternalInput").ap()
            for name, a in arrays.items()}
    out = nc.dram_tensor("out", (TT, P, D), F32, kind="ExternalOutput").ap()
    hybrid_layer(nc, out=out, **args)
    result = run_bass_kernel_spmd(nc, [arrays], core_ids=[0])
    return result.results[0]["out"].reshape(1, SEQ, D)
```
